# Optimizing a Trainium2 kernel written in Bass

```python
import jax, jax.numpy as jnp
from jax import lax
import numpy as np

D_MODEL = 1024
BATCH = 1
SEQ = 1024
DEPTH = 1
DEC_BATCH = 1
DEC_SEQ = 256
PAST_LEN = 128

D_MIX = D_MODEL
D_CONV = D_MIX // 2
D_FOURIER = D_MIX - D_CONV
CONV_HEADS = 8
FOURIER_GROUPS = 8
FOURIER_GROUP_DIM = D_FOURIER // FOURIER_GROUPS
CONV_WIDTH = 3
CONV_PAD = (CONV_WIDTH - 1) // 2
D_IN = 3 * D_CONV + D_FOURIER
N_EXPERTS = 16
CAPACITY_FACTOR = 2
D_FF = 2816
EPS = 1e-6

kernel_name = "hybrid_conv_fourier_ec_encoder"

def rmsnorm(x, g):
    xf = x.astype(jnp.float32)
    var = jnp.mean(xf * xf, axis=-1, keepdims=True)
    return (xf * lax.rsqrt(var + EPS) * g.astype(jnp.float32)).astype(x.dtype)

def short_conv_mixer(u_b, u_c, u_x, conv_w):
    v = u_c * u_x
    s = v.shape[1]
    vp = jnp.pad(v, ((0, 0), (CONV_PAD, CONV_PAD), (0, 0)))
    y = conv_w[0] * vp[:, 0:s]
    for k in range(1, CONV_WIDTH):
        y = y + conv_w[k] * vp[:, k:k + s]
    return u_b * y

def fourier_mixer(u):
    bn, s, _ = u.shape
    ug = u.reshape(bn, s, FOURIER_GROUPS, FOURIER_GROUP_DIM).astype(jnp.float32)
    f = jnp.fft.fft2(ug, axes=(1, 3), norm="ortho")
    return jnp.real(f).reshape(bn, s, D_FOURIER).astype(u.dtype)

def expert_choice_moe(h, w_router, w_gate, w_up, w_down):
    bn, s, d = h.shape
    t = bn * s
    xt = h.reshape(t, d)
    logits = jnp.einsum("td,de->te", xt.astype(jnp.float32), w_router.astype(jnp.float32))
    aff = jax.nn.softmax(logits, axis=-1)
    cap = CAPACITY_FACTOR * t // N_EXPERTS
    gates, idx = lax.top_k(aff.T, cap)
    xe = jnp.take(xt, idx, axis=0)
    a = jnp.einsum("ecd,edf->ecf", xe, w_gate)
    b = jnp.einsum("ecd,edf->ecf", xe, w_up)
    ye = jnp.einsum("ecf,efd->ecd", jax.nn.silu(a) * b, w_down)
    ye = ye * gates[..., None].astype(ye.dtype)
    out = jnp.zeros_like(xt).at[idx.reshape(-1)].add(ye.reshape(-1, d))
    return out.reshape(bn, s, d)

def encoder_trunk(x, norm_mix, w_in, conv_w, g_conv, g_fourier, w_out,
                  norm_ffn, w_router, w_gate, w_up, w_down, norm_final):
    for l in range(DEPTH):
        h = rmsnorm(x, norm_mix[l])
        u = jnp.einsum("bsd,de->bse", h, w_in[l])
        u_b, u_c, u_x, u_f = jnp.split(u, [D_CONV, 2 * D_CONV, 3 * D_CONV], axis=-1)
        y_conv = rmsnorm(short_conv_mixer(u_b, u_c, u_x, conv_w[l]), g_conv[l])
        y_four = rmsnorm(fourier_mixer(u_f), g_fourier[l])
        y_mix = jnp.concatenate([y_conv, y_four], axis=-1)
        x = x + jnp.einsum("bse,ed->bsd", y_mix, w_out[l])
        x = x + expert_choice_moe(rmsnorm(x, norm_ffn[l]), w_router[l],
                                  w_gate[l], w_up[l], w_down[l])
    return rmsnorm(x, norm_final)

def setup_inputs(seed: int = 0) -> dict:
    key = jax.random.key(seed)
    ks = jax.random.split(key, 16)
    f32 = jnp.float32
    nrm = lambda k, shape, scale: jax.random.normal(k, shape, f32) * scale
    gain = lambda k, shape: 1.0 + 0.02 * jax.random.normal(k, shape, f32)
    return {
        "x_prompt": jax.random.normal(ks[0], (BATCH, SEQ, D_MODEL), f32),
        "x_sample": jax.random.normal(ks[1], (DEC_BATCH, DEC_SEQ, D_MODEL), f32),
        "norm_mix": gain(ks[2], (DEPTH, D_MODEL)),
        "w_in": nrm(ks[3], (DEPTH, D_MODEL, D_IN), D_MODEL ** -0.5),
        "conv_w": nrm(ks[4], (DEPTH, CONV_WIDTH, D_CONV), CONV_WIDTH ** -0.5),
        "g_conv": gain(ks[5], (DEPTH, D_CONV)),
        "g_fourier": gain(ks[6], (DEPTH, D_FOURIER)),
        "w_out": nrm(ks[7], (DEPTH, D_MIX, D_MODEL), D_MIX ** -0.5),
        "norm_ffn": gain(ks[8], (DEPTH, D_MODEL)),
        "w_router": nrm(ks[9], (DEPTH, D_MODEL, N_EXPERTS), D_MODEL ** -0.5),
        "w_gate": nrm(ks[10], (DEPTH, N_EXPERTS, D_MODEL, D_FF), D_MODEL ** -0.5),
        "w_up": nrm(ks[11], (DEPTH, N_EXPERTS, D_MODEL, D_FF), D_MODEL ** -0.5),
        "w_down": nrm(ks[12], (DEPTH, N_EXPERTS, D_FF, D_MODEL), D_FF ** -0.5),
        "norm_final": gain(ks[13], (D_MODEL,)),
    }

def reference(x_prompt, x_sample, norm_mix, w_in, conv_w, g_conv, g_fourier, w_out,
              norm_ffn, w_router, w_gate, w_up, w_down, norm_final):
    y_prompt = encoder_trunk(x_prompt, norm_mix, w_in, conv_w, g_conv, g_fourier, w_out,
                             norm_ffn, w_router, w_gate, w_up, w_down, norm_final)
    y_sample = encoder_trunk(x_sample, norm_mix, w_in, conv_w, g_conv, g_fourier, w_out,
                             norm_ffn, w_router, w_gate, w_up, w_down, norm_final)
    return (y_prompt, y_sample)


_drawn_inputs = setup_inputs


def setup_inputs(seed=0):
    import zlib

    import numpy as np

    out = dict(_drawn_inputs(seed))
    spreads = {}
    factors = {'g_conv': 4.461, 'g_fourier': 4.509, 'norm_ffn': 5.091, 'norm_final': 2.739}
    for name, (base, spread) in spreads.items():
        noise = np.random.default_rng([zlib.crc32(name.encode()), seed]).standard_normal(out[name].shape)
        drawn = base * np.exp(spread * noise) if base else spread * noise
        out[name] = __import__('jax').numpy.asarray(drawn.astype(out[name].dtype))
    for name, factor in factors.items():
        out[name] = (out[name] * factor).astype(out[name].dtype)
    return out
```

```python
from contextlib import ExitStack

import concourse.bass as bass
import numpy as np
from concourse import mybir

F32 = mybir.dt.float32
F32R = mybir.dt.float32r
U32 = mybir.dt.uint32
ALU = mybir.AluOpType
ACT = mybir.ActivationFunctionType
AX_X = mybir.AxisListType.X

P = 128
D = 1024
SEQ, DEC = 1024, 256
T = SEQ + DEC
TILES = T // P
DH = D // 2
GROUP = 64
KD = D // P
JH = DH // P
E = 16
F = 2816
FB = F // P
NC = FB // 2
CAP, CAPS = 2 * SEQ // E, 2 * DEC // E
C = CAP + CAPS
UNITS = 3 * NC
UNIT = 2 * D
RAW = 11
SPL = 3
EPS = 1e-6
HE = SEQ // 4 + 2
HO = SEQ // 4
SE = DEC // 4 + 2
SO = DEC // 4
LARGE = 2 * HE + 2 * HO
SMALL = 2 * SE + 2 * SO
HB = SEQ // 2 // P
AB_T = T


def build(nc, x, norm_mix, w_in, conv_w, g_conv, g_fourier, w_out, norm_ffn, w_router, w_gate, w_up, w_down,
          norm_final, dft_d, dft_s, out):
    acc = nc.dram_tensor("acc_dram", (T, D), F32).ap()
    xn_d = nc.dram_tensor("xn_dram", (T, D), F32).ap()
    x_t = x.rearrange("(t p) d -> t p d", p=P)
    acc_t = acc.rearrange("(t p) d -> t p d", p=P)
    xn_t = xn_d.rearrange("(t p) d -> t p d", p=P)
    out_t = out.rearrange("(t p) d -> t p d", p=P)
    win_v = w_in[0].rearrange("(k p) e -> p k e", p=P)
    win_v2 = w_in[0].rearrange("(k p) (a j l c) -> j p k a l c", p=P, a=4, j=2, l=2)
    wout_v = w_out[0].rearrange("(k p) d -> k p d", p=P)
    gate_v = w_gate[0].rearrange("e (k p) f -> e p k f", p=P)
    up_v = w_up[0].rearrange("e (k p) f -> e p k f", p=P)
    down_v = w_down[0].rearrange("e (b p) d -> e p b d", p=P)

    with ExitStack() as ctx:
        base = 16512

        def at(name, offset, shape, dt=F32):
            return nc.alloc_sbuf_tensor_at(name, shape, dt, offset=base + offset)

        def sem(name):
            return ctx.enter_context(nc.semaphore(name))

        KB = 1024
        hT_h = at("hT_h", 0, [P, KD, T], F32R)
        hT_l = at("hT_l", 40 * KB, [P, KD, T], F32R)
        Y_h = at("Y_h", 0, [P, JH, TILES, 2 * P], F32R)
        Y_l = at("Y_l", 40 * KB, [P, JH, TILES, 2 * P], F32R)
        yconv = at("yconv", 80 * KB, [P, JH, T])
        AB_h = at("AB_h", 100 * KB, [P, JH, T], F32R)
        AB_l = at("AB_l", 120 * KB, [P, JH, T], F32R)
        yfour = at("yfour", 120 * KB, [P, JH, T])
        xt = at("xt", 80 * KB, [P, TILES, D])
        xs = at("xs", 120 * KB, [P, 2, D])
        sqj = at("sqj", 128 * KB, [P, D])
        dd = at("dd", 204 * KB + 256, [P, 2, 2 * P], F32R)
        win_raw = at("win_raw", 140 * KB, [P, 2, KD, P])
        win_h = at("win_h", 148 * KB, [P, 2, KD, P], F32R)
        win_l = at("win_l", 156 * KB, [P, 2, KD, P], F32R)
        VW = T + 4
        uc = at("uc", 164 * KB, [P, T])
        v = at("v", 169 * KB, [P, VW])
        tc = at("tc", 175 * KB, [P, T + 2])
        qc = at("qc", 181 * KB, [P, T])
        sqc = at("sqc", 186 * KB, [P, T])
        woc_h = at("woc_h", 140 * KB, [P, JH, D], F32R)
        woc_l = at("woc_l", 156 * KB, [P, JH, D], F32R)
        tab_h = at("tab_h", 172 * KB, [P, HB, LARGE], F32R)
        tab_l = at("tab_l", 172 * KB + HB * LARGE * 4, [P, HB, LARGE], F32R)
        tsm = at("tsm", 100 * KB, [P, 2, SMALL], F32R)
        qf = at("qf", 103 * KB, [P, T])
        sqf = at("sqf", 108 * KB, [P, T])
        qcp = at("qcp", 113 * KB, [P, HE + HO + SE + SO])
        wo_raw = at("wo_raw", 116 * KB, [P, 2, DH])
        wof_h = at("wof_h", 0, [P, JH, D], F32R)
        wof_l = at("wof_l", 40 * KB, [P, JH, D], F32R)
        ysh = at("ysh", 16 * KB, [P, 2, KD, P], F32R)
        ysl = at("ysl", 24 * KB, [P, 2, KD, P], F32R)
        xr = at("xr", 32 * KB, [P, 2, D])
        xn = at("xn", 56 * KB, [P, 2, D])
        xnT = at("xnT", 64 * KB, [P, KD, P])
        gffn = at("gffn", 68 * KB, [P, D])
        sq2 = at("sq2", 72 * KB, [P, D])
        aff = at("aff", 76 * KB, [P, 3, TILES, E])
        A = at("A", 80 * KB, [48, SEQ])
        vals = at("vals", 84 * KB, [48, CAP])
        idx = at("idx", 85 * KB, [48, CAP], U32)
        idxf = at("idxf", 86 * KB, [48, CAP])
        raw = at("raw", 117 * KB, [P, RAW, UNIT])
        spl_h = at("spl_h", 0, [P, SPL, UNIT], F32R)
        spl_l = at("spl_l", 24 * KB, [P, SPL, UNIT], F32R)
        GB = 2 * C
        g = at("g", 48 * KB, [P, FB * GB + 64], F32R)
        xT = at("xT", 76 * KB, [P, KD, 2 * C], F32R)
        xg = at("xg", 86 * KB, [P, D])
        xgs = at("xgs", 90 * KB, [CAPS, D])
        yP = at("yP", 94 * KB, [P, D])
        yS = at("yS", 98 * KB, [CAPS, D])
        slo = at("slo", 102 * KB, [CAPS, D])
        yS2 = at("yS2", 106 * KB, [CAPS, D])
        glo = at("glo", 110 * KB, [P, 2, C])
        av = at("av", 110 * KB + 1280, [P, 2, C])
        sv = at("sv", 110 * KB + 2560, [P, 2, C])
        ulo = at("ulo", 110 * KB + 3840, [P, 2, C])
        bv = at("bv", 110 * KB + 5120, [P, 2, C])
        pv = at("pv", 205 * KB, [P, 2, C])
        fx = at("fx", 117 * KB, [P, TILES, D])
        fo = at("fo", 0, [P, TILES, D])
        fsq = at("fsq", 48 * KB, [P, D])
        gfin = at("gfin", 52 * KB, [P, D])
        M0 = 116 * KB + 256
        M1 = 206 * KB + 512
        ident = at("ident", M1, [P, P])
        gmix = at("gmix", M1 + 512, [P, KD])
        gm2 = at("gm2", M1 + 544, [P, KD])
        cw = at("cw", M1 + 576, [P, 3, JH])
        ones = at("ones", M1 + 640, [P, 2])
        eps = at("eps", M1 + 1312, [P, 1])
        rt2 = at("rt2", M1 + 1344, [P, 2])
        ss = at("ss", M1 + 672, [P, 4])
        rr = at("rr", M1 + 704, [P, 4])
        rn = at("rn", M1 + 736, [P, 2, TILES])
        rm = at("rm", M1 + 832, [P, 2, TILES])
        idxT = at("idxT", M1 + 928, [P, 48], U32)
        gateT = at("gateT", M1 + 1120, [P, 48])
        wr = at("wr", 77 * KB + 896, [P, KD, E])
        gidx = at("gidx", M0, [P, 2], U32)
        sidx = at("sidx", M0 + 32, [P, 2], U32)
        cgate = at("cgate", M0 + 64, [P, 2])
        mx = at("mx", M0 + 96, [P, TILES])
        sm = at("sm", M0 + 160, [P, TILES])
        fss = at("fss", M0 + 224, [P, 2 * TILES])
        frr = at("frr", M0 + 320, [P, TILES])

        ps = ctx.enter_context(nc.psum_tensor("ps", [P, 8, 512], F32))
        psf = ps[:, :, :].rearrange("p b n -> p (b n)")

        def bank(b, n=1):
            return psf[:, b * 512:(b + n) * 512]

        const_in = sem("const_in")
        gffn_in = sem("gffn_in")
        dd_in = sem("dd_in")
        tab_in = sem("tab_in")
        ident_ok = sem("ident_ok")
        x_in = [sem(f"x_in{t}") for t in range(TILES)]
        x_sq = sem("x_sq")
        x_rt = sem("x_rt")
        x_r = sem("x_r")
        xs_ok = sem("xs_ok")
        xT_ps = sem("xT_ps")
        hTh_ok = sem("hTh_ok")
        hTl_ok = sem("hTl_ok")
        win_in = [sem(f"win_in{s}") for s in range(2)]
        winh_ok = sem("winh_ok")
        winl_ok = sem("winl_ok")
        u_done = sem("u_done")
        uc_ok = sem("uc_ok")
        pad_ok = sem("pad_ok")
        v_ok = sem("v_ok")
        t_ok = sem("t_ok")
        ty_ok = sem("ty_ok")
        y_ok = sem("y_ok")
        q_ok = sem("q_ok")
        qs_ok = sem("qs_ok")
        tmp_ok = sem("tmp_ok")
        ab_ok = sem("ab_ok")
        abh_ok = sem("abh_ok")
        abl_ok = sem("abl_ok")
        nrm_ps = sem("nrm_ps")
        rn_a = sem("rn_a")
        rn_rt = sem("rn_rt")
        dd_done = sem("dd_done")
        Yh_ok = sem("Yh_ok")
        Yl_ok = sem("Yl_ok")
        ds_done = sem("ds_done")
        qcp_ok = sem("qcp_ok")
        yf_ok = sem("yf_ok")
        qf_ok = sem("qf_ok")
        qfs_ok = sem("qfs_ok")
        wo_in = [sem(f"wo_in{s}") for s in range(2)]
        woh_ok = sem("woh_ok")
        wol_ok = sem("wol_ok")
        r_in = [sem(f"r_in{s}") for s in range(2)]
        ysh_ok = sem("ysh_ok")
        ysl_ok = sem("ysl_ok")
        oc_done = sem("oc_done")
        of_done = sem("of_done")
        x1_ok = sem("x1_ok")
        x2_ok = sem("x2_ok")
        ss_ok = sem("ss_ok")
        rt_ok = sem("rt_ok")
        rr_ok = sem("rr_ok")
        xn_ok = sem("xn_ok")
        acc_out = [sem(f"acc_out{s}") for s in range(2)]
        xn_out = [sem(f"xn_out{s}") for s in range(2)]
        nT_ps = sem("nT_ps")
        nT_ok = sem("nT_ok")
        lg_ps = sem("lg_ps")
        lg_ok = sem("lg_ok")
        rt_d = sem("rt_d")
        rt_e = sem("rt_e")
        rt_p = sem("rt_p")
        rt_c = sem("rt_c")
        routed = sem("routed")
        raw_in = [sem(f"raw_in{s}") for s in range(RAW)]
        sh_ok = sem("sh_ok")
        sl_ok = sem("sl_ok")
        pe_unit = sem("pe_unit")
        glo_ok = sem("glo_ok")
        a_ok = sem("a_ok")
        s_ok = sem("s_ok")
        ulo_ok = sem("ulo_ok")
        b_ok = sem("b_ok")
        p_ok = sem("p_ok")
        gh_ok = sem("gh_ok")
        gl_ok = sem("gl_ok")
        gpad_ok = sem("gpad_ok")
        gi_ok = sem("gi_ok")
        xg_in = [sem(f"xg_in{s}") for s in range(2)]
        xg_ps = sem("xg_ps")
        xTh_ok = sem("xTh_ok")
        xTl_ok = sem("xTl_ok")
        cg_ok = sem("cg_ok")
        yP_ok = sem("yP_ok")
        slo_ok = sem("slo_ok")
        yS_ok = sem("yS_ok")
        yS2_ok = sem("yS2_ok")
        added = [sem(f"added{s}") for s in range(2)]
        lone = sem("lone")
        f_in = [sem(f"f_in{t}") for t in range(TILES)]
        gfin_in = sem("gfin_in")
        fs_ok = sem("fs_ok")
        frt_ok = sem("frt_ok")
        fr_ok = sem("fr_ok")
        fo_ok = sem("fo_ok")
        f_out = sem("f_out")

        def three(eng, o, a_h, a_l, b_h, b_l, first, last):
            eng.matmul(o, a_h, b_h, start=first, stop=False, skip_group_check=True)
            eng.matmul(o, a_h, b_l, start=False, stop=False, skip_group_check=True)
            return eng.matmul(o, a_l, b_h, start=False, stop=last, skip_group_check=True)

        block = ctx.enter_context(nc.Block())

        @block.sync
        def _(sp):
            sp.dma_start(gmix[:, :], norm_mix[0].rearrange("(k p) -> p k", p=P), allow_slow_non_contiguous=True).then_inc(const_in, 16)
            sp.dma_start(gm2[:, 0:JH], g_conv[0].rearrange("(k p) -> p k", p=P), allow_slow_non_contiguous=True).then_inc(const_in, 16)
            sp.dma_start(gm2[:, JH:KD], g_fourier[0].rearrange("(k p) -> p k", p=P), allow_slow_non_contiguous=True).then_inc(const_in, 16)
            for i in range(3):
                sp.dma_start(cw[:, i, :], conv_w[0, i].rearrange("(k p) -> p k", p=P), allow_slow_non_contiguous=True).then_inc(const_in, 16)

            for t in range(TILES):
                sp.dma_start(xt[:, t, :], x_t[t]).then_inc(x_in[t], 16)

            with sp.Fori(0, 2) as jj:
                for q in range(6):
                    sp.wait_ge(winl_ok, jj * 6 + q + 1)
                    sp.sem_inc(lone, 1)
                    sp.dma_start(win_raw[:, q % 2, :, :],
                                 win_v2[jj, :, :, (1, 2, 0)[q % 3], q // 3, :]).then_inc(win_in[q % 2], 16)
            for j in range(JH):
                sp.wait_ge(winl_ok, 12 + j + 1)
                sp.dma_start(win_raw[:, j % 2, :, :],
                             win_v[:, :, 3 * DH + P * j:3 * DH + P * (j + 1)]).then_inc(win_in[j % 2], 16)

            for n in range(2 * KD):
                if n < 2:
                    sp.wait_ge(dd_done, TILES)
                else:
                    sp.wait_ge(wol_ok, n - 1)
                sp.dma_start(wo_raw[:, n % 2, :], wout_v[n // 2][:, (n % 2) * DH:(n % 2 + 1) * DH]).then_inc(wo_in[n % 2], 16)

            sp.wait_ge(ds_done, 3 * JH)
            sp.dma_start(gffn[:, :], norm_ffn.partition_broadcast(P)[:, 0, :]).then_inc(gffn_in, 16)
            sp.dma_start(wr[:, :, :], w_router[0].rearrange("(k p) e -> p k e", p=P)).then_inc(gffn_in, 16)
            for s in range(2):
                sp.dma_start(xr[:, s, :], x_t[s]).then_inc(r_in[s], 16)
            with sp.Fori(0, TILES // 2 - 1) as tb:
                for s in range(2):
                    sp.wait_ge(x2_ok, tb * 2 + s + 2)
                    sp.dma_start(acc_t[tb * 2 + s], xr[:, s, :]).then_inc(acc_out[s], 16)
                    sp.wait_ge(xn_ok, tb * 2 + s + 3)
                    sp.dma_start(xn_t[tb * 2 + s], xn[:, s, :]).then_inc(xn_out[s], 16)
                    sp.wait_ge(acc_out[s], tb * 16 + 32)
                    sp.dma_start(xr[:, s, :], x_t[tb * 2 + s + 2]).then_inc(r_in[s], 16)
            for s in range(2):
                t = TILES - 2 + s
                sp.wait_ge(x2_ok, t + 2)
                sp.dma_start(acc_t[t], xr[:, s, :]).then_inc(acc_out[s], 16)
                sp.wait_ge(xn_ok, t + 3)
                sp.dma_start(xn_t[t], xn[:, s, :]).then_inc(xn_out[s], 16)

            sp.wait_ge(of_done, TILES + 2)
            with sp.Fori(0, E) as e:
                for i in range(UNITS):
                    sp.wait_ge(sl_ok, e * UNITS + (i + 1))
                    if i < 2 * NC:
                        w = (gate_v, up_v)[i % 2]
                        src = w[e, :, :, (i // 2) * 2 * P:(i // 2 + 1) * 2 * P]
                        dst = raw[:, i % RAW, :].rearrange("p (k f) -> p k f", k=KD)
                    else:
                        j = i - 2 * NC
                        src = down_v[e, :, 2 * j:2 * j + 2, :]
                        dst = raw[:, i % RAW, :].rearrange("p (b d) -> p b d", b=2)
                    sp.dma_start(dst, src).then_inc(raw_in[i % RAW], 16)

            sp.wait_ge(sl_ok, RAW + E * UNITS)
            sp.wait_ge(gl_ok, 2 * E * NC)
            sp.wait_ge(pe_unit, E * UNITS)
            sp.dma_start(gfin[:, :], norm_final.partition_broadcast(P)).then_inc(gfin_in, 16)
            sp.wait_ge(added[0], 16 * E)
            sp.wait_ge(added[1], 16 * E)
            for t in range(TILES):
                sp.dma_start(fx[:, t, :], acc_t[t]).then_inc(f_in[t], 16)
            for t in range(TILES):
                sp.wait_ge(fo_ok, t + 1)
                sp.dma_start(out_t[t], fo[:, t, :]).then_inc(f_out, 16)
            sp.wait_ge(f_out, 16 * TILES)

        @block.gpsimd
        def _(pool):
            for s, n in ((winl_ok, 2), (u_done, 2), (v_ok, 1), (y_ok, 1), 
                         (of_done, 2), (x1_ok, 1), (x2_ok, 1), (xn_ok, 2), (nT_ps, 2), (lg_ps, 1),
                         (acc_out[0], 16), (acc_out[1], 16), (xn_out[0], 16), (xn_out[1], 16),
                         (sl_ok, RAW), (yS_ok, 1)):
                pool.sem_inc(s, n)
            pool.memset(ident[:, :], 0.0).then_inc(ident_ok, 1)
            pool.memset(ones[:, :], 1.0).then_inc(ident_ok, 1)
            pool.memset(eps[:, :], EPS).then_inc(ident_ok, 1)
            pool.wait_ge(ident_ok, 3)
            pool.affine_select(out=ident[:, :], in_=ident[:, :], compare_op=ALU.not_equal, fill=1.0, base=0,
                               pattern=[[-1, P]], channel_multiplier=1).then_inc(ident_ok, 1)
            pool.memset(v[:, :], 0.0).then_inc(pad_ok, 1)
            pool.memset(qc[:, :], 0.0).then_inc(pad_ok, 1)
            pool.wait_ge(pad_ok, 2)
            pool.dma_start(dd[:, :, :], dft_d.rearrange("p (h n) -> p h n", h=2)).then_inc(dd_in, 16)
            with pool.Fori(0, JH) as j:
                pool.wait_ge(y_ok, j + 2)
                pool.tensor_tensor(sqc[:, :], yconv[:, j, :], yconv[:, j, :], ALU.mult).then_inc(qs_ok, 1)
                pool.wait_ge(qs_ok, j * 2 + 1)
                pool.tensor_tensor(qc[:, :], qc[:, :], sqc[:, :], ALU.add).then_inc(qs_ok, 1)
                pool.wait_ge(qs_ok, j * 2 + 2)
            pool.sem_inc(q_ok, 1)
            pool.wait_ge(u_done, 2 + 16)
            pool.wait_ge(abl_ok, JH)
            pool.wait_ge(nrm_ps, 1)
            sv_ = dft_s.rearrange("h p n -> p h n")
            pool.dma_start(tab_h[:, :, :].rearrange("p b n -> p (b n)"), sv_[:, 0, 0:HB * LARGE]).then_inc(tab_in, 16)
            pool.dma_start(tab_l[:, :, :].rearrange("p b n -> p (b n)"), sv_[:, 1, 0:HB * LARGE]).then_inc(tab_in, 16)
            pool.wait_ge(dd_done, TILES)
            pool.dma_start(tsm[:, :, :], sv_[:, :, HB * LARGE:]).then_inc(tab_in, 16)
            pool.memset(qf[:, :], 0.0).then_inc(qfs_ok, 1)
            pool.wait_ge(qfs_ok, 1)
            for j in range(JH):
                pool.wait_ge(yf_ok, 8 * (j + 1))
                pool.tensor_tensor(sqf[:, :], yfour[:, j, :], yfour[:, j, :], ALU.mult).then_inc(qfs_ok, 1)
                pool.wait_ge(qfs_ok, 2 * j + 2)
                pool.tensor_tensor(qf[:, :], qf[:, :], sqf[:, :], ALU.add).then_inc(qfs_ok, 1)
                pool.wait_ge(qfs_ok, 2 * j + 3)
            pool.sem_inc(qf_ok, 1)

            def gather(e, prior):
                if prior is not None:
                    pool.wait_ge(xg_ps, prior)
                pool.tensor_copy(gidx[:, 0:1], idxT[:, bass.ds(e, 1)]).then_inc(gi_ok, 1)
                pool.tensor_copy(gidx[:, 1:2], idxT[:, bass.ds(e + 32, 1)]).then_inc(gi_ok, 1)
                pool.wait_ge(gi_ok, e * 2 + 2)
                pool.sem_inc(lone, 1)
                pool.indirect_dma_start(xg[:, :], None, xn_d,
                                        bass.IndirectOffsetOnAxis(gidx[:, 0:1], 0)).then_inc(xg_in[0], 16)
                pool.indirect_dma_start(xgs[:, :], None, xn_d,
                                        bass.IndirectOffsetOnAxis(gidx[0:CAPS, 1:2], 0)).then_inc(xg_in[1], 16)

            def scatter(e, first=False):
                if not first:
                    pool.wait_ge(added[0], e * 16)
                    pool.wait_ge(added[1], e * 16)
                pool.tensor_copy(sidx[:, 0:1], idxT[:, bass.ds(e, 1)]).then_inc(cg_ok, 1)
                pool.tensor_copy(sidx[:, 1:2], idxT[:, bass.ds(e + 32, 1)]).then_inc(cg_ok, 1)
                pool.tensor_copy(cgate[:, 0:1], gateT[:, bass.ds(e, 1)]).then_inc(cg_ok, 1)
                pool.tensor_copy(cgate[:, 1:2], gateT[:, bass.ds(e + 32, 1)]).then_inc(cg_ok, 1)
                pool.wait_ge(cg_ok, e * 4 + 4)
                pool.wait_ge(yS_ok, e + 2)
                pool.sem_inc(lone, 1)
                pool.tensor_scalar(yS2[:, :], yS[:, :], cgate[0:CAPS, 1:2], None, ALU.mult).then_inc(yS2_ok, 1)
                pool.wait_ge(yP_ok, e + 1)
                pool.sem_inc(lone, 1)
                pool.indirect_dma_start(acc, bass.IndirectOffsetOnAxis(sidx[:, 0:1], 0), yP[:, :], None,
                                        compute_op=ALU.add).then_inc(added[0], 16)
                pool.wait_ge(yS2_ok, e + 1)
                pool.sem_inc(lone, 1)
                pool.indirect_dma_start(acc, bass.IndirectOffsetOnAxis(sidx[0:CAPS, 1:2], 0), yS2[:, :], None,
                                        compute_op=ALU.add).then_inc(added[1], 16)

            pool.wait_ge(routed, 1)
            for s in range(2):
                pool.wait_ge(xn_out[s], 16 * (TILES // 2 + 1))
                pool.wait_ge(acc_out[s], 16 * (TILES // 2 + 1))
            pool.memset(g[:, FB * GB:].bitcast(F32), 0.0).then_inc(gpad_ok, 1)
            gather(0, None)
            gather(1, 1)
            scatter(0, True)
            with pool.Fori(1, E - 1) as e:
                gather(e + 1, e + 1)
                scatter(e)
            scatter(E - 1)

        @block.scalar
        def _(act):
            act.wait_ge(ident_ok, 4)
            def square_x(t):
                s = t % 2
                act.wait_ge(x_in[t], 16)
                if t >= 2:
                    act.wait_ge(xs_ok, t - 1)
                act.activation(sqj[:, :], xt[:, t, :], ACT.Square, accum_out=ss[:, s:s + 1]).then_inc(x_sq, 1)
                act.wait_ge(x_sq, t + 1)
                act.activation(rm[:, 0, s:s + 1], ss[:, s:s + 1], ACT.Sqrt, bias=eps[:, 0:1], scale=1.0 / D).then_inc(x_rt, 1)

            square_x(0)
            square_x(1)
            for t in range(TILES):
                if t + 2 < TILES:
                    square_x(t + 2)
                act.wait_ge(xT_ps, t + 1)
                act.activation(hT_h[:, :, t * P:(t + 1) * P],
                               bank(2 * (t % 2), 2).rearrange("p (k t) -> p k t", k=KD), ACT.Copy).then_inc(hTh_ok, 1)

            act.wait_ge(const_in, 96)

            def win_hi(n, slot, landed):
                act.wait_ge(win_in[slot], landed)
                act.wait_ge(u_done, n + 1)
                for k in range(KD):
                    last = act.activation(win_h[:, slot, k, :], win_raw[:, slot, k, :], ACT.Copy, scale=gmix[:, k:k + 1])
                last.then_inc(winh_ok, 1)

            win_hi(0, 0, 16)
            with act.Fori(0, 2) as jj:
                for q in range(6):
                    n, j = jj * 6 + q, jj * 2 + q // 3
                    win_hi(n + 1, (q + 1) % 2, jj * 48 + 16 * ((q + 1) // 2 + 1))
                    if q % 3 == 0:
                        act.wait_ge(u_done, n + 3)
                        act.wait_ge(v_ok, j + 1)
                        act.activation(uc[:, :], bank(3 * (q % 2), 3)[:, 0:T], ACT.Copy).then_inc(uc_ok, 1)
                    if q % 3 == 1:
                        act.wait_ge(v_ok, j + 2)
                        act.wait_ge(y_ok, j + 1)
                        act.activation(tc[:, :], v[:, 0:T + 2], ACT.Copy, scale=cw[:, 0, bass.ds(j, 1)]).then_inc(t_ok, 1)
            for j in range(JH):
                n = 12 + j
                if j < JH - 1:
                    win_hi(n + 1, (n + 1) % 2, 16 * ((n + 1) // 2 + 1))
                act.wait_ge(u_done, n + 3)
                if j == 0:
                    act.wait_ge(v_ok, JH + 1)
                else:
                    act.wait_ge(ab_ok, 4 * j)
                u = bank(3 * (n % 2), 3)
                act.activation(uc[:, 0:SEQ // 2], u[:, SEQ // 2:SEQ], ACT.Copy).then_inc(tmp_ok, 1)
                act.activation(uc[:, SEQ // 2:SEQ // 2 + DEC // 2], u[:, SEQ + DEC // 2:T], ACT.Copy).then_inc(tmp_ok, 1)
                act.wait_ge(ab_ok, 4 * (j + 1))
                act.activation(AB_h[:, j, :], tc[:, 0:T], ACT.Copy).then_inc(abh_ok, 1)

            act.wait_ge(nrm_ps, 1)
            act.activation(rm[:, 0, :], bank(7)[:, 0:TILES], ACT.Sqrt, bias=eps[:, 0:1], scale=1.0 / DH).then_inc(rn_rt, 1)

            act.wait_ge(abl_ok, JH)
            for t in range(TILES):
                act.wait_ge(dd_done, t + 1)
                act.activation(Y_h[:, :, t, :], bank(2 * (t % 2), 2).rearrange("p (j c) -> p j c", j=JH),
                               ACT.Copy).then_inc(Yh_ok, 1)

            def wo_hi(n):
                k, h = n // 2, n % 2
                act.wait_ge(wo_in[n % 2], 16 * (n // 2 + 1))
                dst = woc_h if k < JH else wof_h
                act.activation(dst[:, k % JH, h * DH:(h + 1) * DH], wo_raw[:, n % 2, :], ACT.Copy,
                               scale=gm2[:, k:k + 1]).then_inc(woh_ok, 1)

            act.wait_ge(u_done, 2 + 16)
            act.wait_ge(nrm_ps, 1)
            for j in range(JH):
                for i, (b, o, w) in enumerate(((5, 0, HE), (7, HE, HO))):
                    act.wait_ge(ds_done, 3 * j + i + 1)
                    if j:
                        act.wait_ge(yf_ok, 8 * (j - 1) + 2 * (i + 1))
                    act.activation(qcp[:, o:o + w], bank(b)[:, 0:w], ACT.Copy).then_inc(qcp_ok, 1)
                    wo_hi(4 * j + 2 * i)
                    wo_hi(4 * j + 2 * i + 1)
                act.wait_ge(ds_done, 3 * j + 3)
                if j:
                    act.wait_ge(yf_ok, 8 * j)
                act.activation(qcp[:, HE + HO:HE + HO + SE], bank(3)[:, SE:2 * SE], ACT.Copy).then_inc(qcp_ok, 1)
                act.activation(qcp[:, HE + HO + SE:], bank(3)[:, 2 * SE + SO:SMALL], ACT.Copy).then_inc(qcp_ok, 1)

            def stage_hi(t, s):
                act.wait_ge(of_done, t + 1)
                if isinstance(t, int) and t == 0:
                    act.wait_ge(ds_done, 3 * JH)
                for h, y in enumerate((yconv, yfour)):
                    act.activation(ysh[:, s, JH * h:JH * (h + 1), :], y[:, :, bass.ds(t * P, P)], ACT.Copy).then_inc(ysh_ok, 1)

            def rows(t, s, before, after):
                if after:
                    stage_hi(t + 1, 1 - s)
                if before:
                    act.wait_ge(nT_ps, t + 2)
                    act.wait_ge(lg_ps, t)
                    act.activation(xnT[:, :, :], bank(4, 2).rearrange("p (k t) -> p k t", k=KD), ACT.Copy).then_inc(nT_ok, 1)
                if before != "end":
                    act.wait_ge(x2_ok, t + 2)
                    act.activation(sq2[:, :], xr[:, s, :], ACT.Square, accum_out=ss[:, 2 + s:3 + s]).then_inc(ss_ok, 1)
                    act.wait_ge(ss_ok, t + 1)
                    act.activation(rt2[:, s:s + 1], ss[:, 2 + s:3 + s], ACT.Sqrt, bias=eps[:, 0:1], scale=1.0 / D).then_inc(rt_ok, 1)

            act.wait_ge(yf_ok, 8 * JH)
            stage_hi(0, 0)
            act.wait_ge(nrm_ps, 2)
            act.activation(rm[:, 1, :], bank(7)[:, 16:16 + TILES], ACT.Sqrt, bias=eps[:, 0:1], scale=1.0 / DH).then_inc(rn_rt, 1)
            rows(0, 0, False, True)
            with act.Fori(0, TILES // 2 - 1) as tb:
                rows(tb * 2 + 1, 1, True, True)
                rows(tb * 2 + 2, 0, True, True)
            rows(TILES - 1, 1, True, False)
            rows(TILES, 0, "end", False)

            act.wait_ge(rt_d, 2)
            act.activation(aff[:, 1, :, :], aff[:, 0, :, :], ACT.Exp).then_inc(rt_e, 1)
            act.wait_ge(rt_p, 1)
            act.wait_ge(rt_c, 1)
            act.activation(A[0:E, :], ps[0:E, 0:2, :].rearrange("p b n -> p (b n)"), ACT.Copy).then_inc(rt_e, 1)
            act.activation(A[32:32 + E, 0:DEC], ps[0:E, 2, 0:DEC], ACT.Copy).then_inc(rt_e, 1)

            def split_hi(e, i):
                act.wait_ge(raw_in[i % RAW], e * (16 * UNITS // RAW) + 16 * (i // RAW + 1))
                if isinstance(e, int) and e == 0 and i < SPL:
                    act.wait_ge(routed, 1)
                else:
                    act.wait_ge(pe_unit, e * UNITS + (i - SPL + 1))
                act.activation(spl_h[:, i % SPL, :], raw[:, i % RAW, :], ACT.Copy).then_inc(sh_ok, 1)

            def gathered_hi(n):
                act.wait_ge(xg_ps, n)
                act.activation(xT[:, :, 0:C].rearrange("p (b k) c -> p b k c", b=4),
                               ps[:, 0:4, 0:2 * C].rearrange("p b (k c) -> p b k c", k=2), ACT.Copy).then_inc(xTh_ok, 1)

            def after_unit(e, i):
                if i < 2 * NC and i % 2 == 0:
                    c = i // 2
                    act.wait_ge(pe_unit, e * UNITS + (i + 1))
                    if not (isinstance(e, int) and e == 0 and c == 0):
                        act.wait_ge(a_ok, e * NC + c)
                    act.activation(glo[:, :, :], ps[:, 0:2, C:2 * C], ACT.Copy).then_inc(glo_ok, 1)
                elif i < 2 * NC:
                    c = i // 2
                    act.wait_ge(a_ok, e * NC + (c + 1))
                    if not (isinstance(e, int) and e == 0 and c == 0):
                        act.wait_ge(p_ok, e * NC + c)
                    act.activation(sv[:, :, :], av[:, :, :], ACT.Silu).then_inc(s_ok, 1)
                    act.wait_ge(pe_unit, e * UNITS + (i + 1))
                    if not (isinstance(e, int) and e == 0 and c == 0):
                        act.wait_ge(b_ok, e * NC + c)
                    act.activation(ulo[:, :, :], ps[:, 2:4, C:2 * C], ACT.Copy).then_inc(ulo_ok, 1)
                elif i == UNITS - 1:
                    act.wait_ge(pe_unit, e * UNITS + UNITS)
                    act.wait_ge(cg_ok, e * 4 + 4)
                    act.activation(yP[:, :], bank(4, 2), ACT.Copy, scale=cgate[:, 0:1]).then_inc(yP_ok, 1)
                    act.wait_ge(yS_ok, e + 1)
                    act.activation(slo[:, :], ps[32:64, 6:8, :].rearrange("p b n -> p (b n)"), ACT.Copy).then_inc(slo_ok, 1)

            def product_hi(e, i):
                if i < 2 * NC and i % 2:
                    c = i // 2
                    act.wait_ge(p_ok, e * NC + (c + 1))
                    gb = g[:, 2 * c * GB:(2 * c + 2) * GB].rearrange("p (b n) -> p b n", b=2)
                    act.activation(gb[:, :, P:P + C], pv[:, :, :], ACT.Copy).then_inc(gh_ok, 1)

            def expert(e, last):
                for i in range(1, UNITS + 1):
                    after_unit(e, i - 1)
                    if i == 26 and not last:
                        gathered_hi(e + 2)
                    n = i + SPL - 1
                    if n < UNITS:
                        split_hi(e, n)
                    elif not last:
                        split_hi(e + 1, n - UNITS)
                    product_hi(e, i - 1)

            act.wait_ge(routed, 1)
            for s in range(2):
                act.wait_ge(xn_out[s], 16 * (TILES // 2 + 1))
            gathered_hi(1)
            for i in range(SPL):
                split_hi(0, i)
            expert(0, False)
            with act.Fori(1, E - 1) as e:
                expert(e, False)
            expert(E - 1, True)

            for t in range(TILES):
                act.wait_ge(f_in[t], 16)
                act.activation(fsq[:, :], fx[:, t, :], ACT.Square, accum_out=fss[:, t:t + 1]).then_inc(fs_ok, 1)
                act.wait_ge(fs_ok, t + 1)
                act.activation(fss[:, TILES + t:TILES + t + 1], fss[:, t:t + 1], ACT.Sqrt, bias=eps[:, 0:1],
                               scale=1.0 / D).then_inc(frt_ok, 1)

        @block.vector
        def _(dve):
            def scale_x(t):
                s = t % 2
                dve.wait_ge(x_rt, t + 1)
                dve.reciprocal(rr[:, s:s + 1], rm[:, 0, s:s + 1]).then_inc(x_r, 1)
                dve.wait_ge(x_r, t + 1)
                if t >= 2:
                    dve.wait_ge(xT_ps, t - 1)
                dve.tensor_scalar(xs[:, s, :], xt[:, t, :], rr[:, s:s + 1], None, ALU.mult).then_inc(xs_ok, 1)

            scale_x(0)
            for t in range(TILES):
                if t + 1 < TILES:
                    scale_x(t + 1)
                dve.wait_ge(hTh_ok, t + 1)
                hs = slice(t * P, (t + 1) * P)
                dve.tensor_tensor(hT_l[:, :, hs], bank(2 * (t % 2), 2).rearrange("p (k t) -> p k t", k=KD),
                                  hT_h[:, :, hs].bitcast(F32), ALU.subtract).then_inc(hTl_ok, 1)

            def win_lo(n, slot):
                dve.wait_ge(winh_ok, n + 1)
                for k in range(KD):
                    last = dve.scalar_tensor_tensor(out=win_l[:, slot, k, :], in0=win_raw[:, slot, k, :],
                                                    scalar=gmix[:, k:k + 1], in1=win_h[:, slot, k, :].bitcast(F32),
                                                    op0=ALU.mult, op1=ALU.subtract)
                last.then_inc(winl_ok, 1)

            dve.wait_ge(const_in, 96)
            dve.wait_ge(pad_ok, 2)
            win_lo(0, 0)
            with dve.Fori(0, 2) as jj:
                for q in range(6):
                    n, j = jj * 6 + q, jj * 2 + q // 3
                    win_lo(n + 1, (q + 1) % 2)
                    u = bank(3 * (q % 2), 3)
                    if q % 3 == 1:
                        dve.wait_ge(u_done, n + 3)
                        dve.wait_ge(uc_ok, j + 1)
                        dve.tensor_tensor(v[:, 1:SEQ + 1], u[:, 0:SEQ], uc[:, 0:SEQ], ALU.mult)
                        dve.tensor_tensor(v[:, SEQ + 3:T + 3], u[:, SEQ:T], uc[:, SEQ:T], ALU.mult).then_inc(v_ok, 1)
                        dve.wait_ge(v_ok, j + 2)
                        dve.wait_ge(t_ok, j + 1)
                        for i in (1, 2):
                            dve.scalar_tensor_tensor(out=tc[:, :], in0=v[:, i:i + T + 2], scalar=cw[:, i, bass.ds(j, 1)],
                                                     in1=tc[:, :], op0=ALU.mult, op1=ALU.add).then_inc(ty_ok, 1)
                            dve.wait_ge(ty_ok, j * 2 + i)
                    if q % 3 == 2:
                        dve.wait_ge(u_done, n + 3)
                        dve.tensor_tensor(yconv[:, j, 0:SEQ], u[:, 0:SEQ], tc[:, 0:SEQ], ALU.mult)
                        dve.tensor_tensor(yconv[:, j, SEQ:T], u[:, SEQ:T], tc[:, SEQ + 2:T + 2], ALU.mult).then_inc(y_ok, 1)
            for j in range(JH):
                n = 12 + j
                if j < JH - 1:
                    win_lo(n + 1, (n + 1) % 2)
                dve.wait_ge(tmp_ok, 2 * (j + 1))
                if j == 0:
                    dve.wait_ge(y_ok, JH + 1)
                else:
                    dve.wait_ge(abl_ok, j)
                u = bank(3 * (n % 2), 3)
                H1, H2 = SEQ // 2, DEC // 2
                for o, u0, t0, w, op in ((0, 0, 0, H1, ALU.add), (H1, 0, 0, H1, ALU.subtract),
                                         (SEQ, SEQ, H1, H2, ALU.add), (SEQ + H2, SEQ, H1, H2, ALU.subtract)):
                    dve.tensor_tensor(tc[:, o:o + w], u[:, u0:u0 + w], uc[:, t0:t0 + w], op).then_inc(ab_ok, 1)
                dve.wait_ge(abh_ok, j + 1)
                dve.tensor_tensor(AB_l[:, j, :], tc[:, 0:T], AB_h[:, j, :].bitcast(F32), ALU.subtract).then_inc(abl_ok, 1)

            dve.wait_ge(rn_rt, 1)
            dve.reciprocal(rn[:, 0, :], rm[:, 0, :]).then_inc(rn_a, 1)

            for t in range(TILES):
                dve.wait_ge(Yh_ok, t + 1)
                dve.tensor_tensor(Y_l[:, :, t, :], bank(2 * (t % 2), 2).rearrange("p (j c) -> p j c", j=JH),
                                  Y_h[:, :, t, :].bitcast(F32), ALU.subtract).then_inc(Yl_ok, 1)

            def wo_lo(n):
                k, h = n // 2, n % 2
                dve.wait_ge(woh_ok, n + 1)
                hi, lo = ((woc_h, woc_l) if k < JH else (wof_h, wof_l))
                cs = slice(h * DH, (h + 1) * DH)
                dve.scalar_tensor_tensor(out=lo[:, k % JH, cs], in0=wo_raw[:, n % 2, :], scalar=gm2[:, k:k + 1],
                                         in1=hi[:, k % JH, cs].bitcast(F32), op0=ALU.mult, op1=ALU.subtract).then_inc(wol_ok, 1)

            for j in range(JH):
                yp, ysm = yfour[:, j, 0:SEQ], yfour[:, j, SEQ:T]
                pairs = ((yp[:, 0:SEQ // 2 + 1:2], yp[:, SEQ - 2:SEQ // 2:-2], bank(4), 0, SEQ // 4 + 1, 1, SEQ // 4),
                         (yp[:, 1:SEQ // 2:2], yp[:, SEQ - 1:SEQ // 2:-2], bank(6), HE, SEQ // 4, 0, SEQ // 4))
                for i, (up_, down_, b, o, w, r0, r1) in enumerate(pairs):
                    dve.wait_ge(qcp_ok, 4 * j + i + 1)
                    dve.tensor_tensor(up_, b[:, 0:w], qcp[:, o:o + w], ALU.subtract).then_inc(yf_ok, 1)
                    dve.tensor_tensor(down_, b[:, r0:r1], qcp[:, o + r0:o + r1], ALU.add).then_inc(yf_ok, 1)
                    wo_lo(4 * j + 2 * i)
                    wo_lo(4 * j + 2 * i + 1)
                dve.wait_ge(qcp_ok, 4 * j + 4)
                o = HE + HO
                b = bank(3)
                H = DEC // 4
                dve.tensor_tensor(ysm[:, 0:DEC // 2 + 1:2], b[:, 0:H + 1], qcp[:, o:o + H + 1], ALU.subtract).then_inc(yf_ok, 1)
                dve.tensor_tensor(ysm[:, DEC - 2:DEC // 2:-2], b[:, 1:H], qcp[:, o + 1:o + H], ALU.add).then_inc(yf_ok, 1)
                o, b = o + SE, b[:, 2 * SE:]
                dve.tensor_tensor(ysm[:, 1:DEC // 2:2], b[:, 0:H], qcp[:, o:o + H], ALU.subtract).then_inc(yf_ok, 1)
                dve.tensor_tensor(ysm[:, DEC - 1:DEC // 2:-2], b[:, 0:H], qcp[:, o:o + H], ALU.add).then_inc(yf_ok, 1)

            def stage_lo(t, s):
                dve.wait_ge(ysh_ok, t * 2 + 2)
                for h, y in enumerate((yconv, yfour)):
                    hs = slice(JH * h, JH * (h + 1))
                    dve.tensor_tensor(ysl[:, s, hs, :], y[:, :, bass.ds(t * P, P)], ysh[:, s, hs, :].bitcast(F32),
                                      ALU.subtract).then_inc(ysl_ok, 1)

            def rows(t, s, before, after):
                if after:
                    stage_lo(t + 1, 1 - s)
                if before != "end":
                    slot_in = t * 8 + (16 - 8 * s)
                    dve.wait_ge(r_in[s], slot_in)
                    dve.wait_ge(oc_done, t + 1)
                    dve.scalar_tensor_tensor(out=xr[:, s, :], in0=bank(0, 2), scalar=rn[:, 0, bass.ds(t, 1)],
                                             in1=xr[:, s, :], op0=ALU.mult, op1=ALU.add).then_inc(x1_ok, 1)
                    dve.wait_ge(x1_ok, t + 2)
                    dve.wait_ge(of_done, t + 3)
                    dve.scalar_tensor_tensor(out=xr[:, s, :], in0=bank(2, 2), scalar=rn[:, 1, bass.ds(t, 1)],
                                             in1=xr[:, s, :], op0=ALU.mult, op1=ALU.add).then_inc(x2_ok, 1)
                    dve.wait_ge(x2_ok, t + 2)
                    dve.wait_ge(rt_ok, t + 1)
                    dve.reciprocal(rr[:, 2 + s:3 + s], rt2[:, s:s + 1]).then_inc(rr_ok, 1)
                    dve.wait_ge(rr_ok, t + 1)
                    dve.wait_ge(nT_ps, t + 1)
                    dve.wait_ge(xn_out[s], slot_in)
                    dve.scalar_tensor_tensor(out=xn[:, s, :], in0=xr[:, s, :], scalar=rr[:, 2 + s:3 + s],
                                             in1=gffn[:, :], op0=ALU.mult, op1=ALU.mult).then_inc(xn_ok, 1)
                if before:
                    dve.wait_ge(lg_ps, t + 1)
                    dve.tensor_copy(aff[:, 0, bass.ds(t - 1, 1), :], bank(6)[:, 0:E]).then_inc(lg_ok, 1)

            stage_lo(0, 0)
            dve.wait_ge(rn_rt, 2)
            dve.reciprocal(rn[:, 1, :], rm[:, 1, :]).then_inc(rn_a, 1)
            dve.wait_ge(rn_a, 2)
            dve.wait_ge(gffn_in, 32)
            rows(0, 0, False, True)
            with dve.Fori(0, TILES // 2 - 1) as tb:
                rows(tb * 2 + 1, 1, True, True)
                rows(tb * 2 + 2, 0, True, True)
            rows(TILES - 1, 1, True, False)
            rows(TILES, 0, "end", False)

            dve.wait_ge(lg_ok, TILES)
            dve.tensor_reduce(mx[:, :], aff[:, 0, :, :], AX_X, ALU.max).then_inc(rt_d, 1)
            dve.wait_ge(rt_d, 1)
            dve.tensor_tensor(aff[:, 0, :, :], aff[:, 0, :, :], mx[:, :].unsqueeze(2).broadcast_to([P, TILES, E]),
                              ALU.subtract).then_inc(rt_d, 1)
            dve.wait_ge(rt_e, 1)
            dve.tensor_reduce(sm[:, :], aff[:, 1, :, :], AX_X, ALU.add).then_inc(rt_d, 1)
            dve.wait_ge(rt_d, 3)
            dve.reciprocal(mx[:, :], sm[:, :]).then_inc(rt_d, 1)
            dve.wait_ge(rt_d, 4)
            dve.tensor_tensor(aff[:, 2, :, :], aff[:, 1, :, :], mx[:, :].unsqueeze(2).broadcast_to([P, TILES, E]),
                              ALU.mult).then_inc(rt_d, 1)
            dve.memset(A[:, :], -1.0).then_inc(rt_c, 1)
            dve.memset(vals[:, :], 0.0).then_inc(rt_d, 1)
            dve.memset(idx[:, :], 0).then_inc(rt_d, 1)
            dve.wait_ge(rt_d, 7)
            dve.wait_ge(rt_e, 3)
            step = 7
            for r in range(CAP // 8):
                n = 48 if r < CAPS // 8 else E
                rs = slice(8 * r, 8 * r + 8)
                dve.max(vals[0:n, rs], A[0:n, :]).then_inc(rt_d, 1)
                dve.wait_ge(rt_d, step + 1)
                dve.max_index(idx[0:n, rs], vals[0:n, rs], A[0:n, :]).then_inc(rt_d, 1)
                dve.wait_ge(rt_d, step + 2)
                dve.match_replace(A[0:n, :], vals[0:n, rs], A[0:n, :], -2.0).then_inc(rt_d, 1)
                dve.wait_ge(rt_d, step + 3)
                step += 3
            dve.tensor_copy(idxf[:, :], idx[:, :]).then_inc(rt_c, 1)
            dve.wait_ge(rt_p, 2)
            dve.tensor_copy(gateT[:, :], bank(3)[:, 0:48])
            dve.tensor_copy(idxT[:, 0:32], bank(3)[:, 48:80])
            dve.tensor_scalar(idxT[:, 32:48], bank(3)[:, 80:96], float(SEQ), None, ALU.add).then_inc(routed, 1)

            def split_lo(e, i):
                dve.wait_ge(sh_ok, e * UNITS + (i + 1))
                dve.tensor_tensor(spl_l[:, i % SPL, :], raw[:, i % RAW, :], spl_h[:, i % SPL, :].bitcast(F32),
                                  ALU.subtract).then_inc(sl_ok, 1)

            def gathered_lo(n):
                dve.wait_ge(xTh_ok, n)
                dve.tensor_tensor(xT[:, :, C:2 * C].rearrange("p (b k) c -> p b k c", b=4),
                                  ps[:, 0:4, 0:2 * C].rearrange("p b (k c) -> p b k c", k=2),
                                  xT[:, :, 0:C].rearrange("p (b k) c -> p b k c", b=4).bitcast(F32),
                                  ALU.subtract).then_inc(xTl_ok, 1)

            def after_unit(e, i):
                c = i // 2
                if i < 2 * NC and i % 2 == 0:
                    dve.wait_ge(glo_ok, e * NC + (c + 1))
                    if not (isinstance(e, int) and e == 0 and c == 0):
                        dve.wait_ge(s_ok, e * NC + c)
                    dve.tensor_tensor(av[:, :, :], ps[:, 0:2, 0:C], glo[:, :, :], ALU.add).then_inc(a_ok, 1)
                elif i < 2 * NC:
                    dve.wait_ge(ulo_ok, e * NC + (c + 1))
                    dve.tensor_tensor(bv[:, :, :], ps[:, 2:4, 0:C], ulo[:, :, :], ALU.add).then_inc(b_ok, 1)
                    dve.wait_ge(b_ok, e * NC + (c + 1))
                    dve.wait_ge(s_ok, e * NC + (c + 1))
                    dve.tensor_tensor(pv[:, :, :], sv[:, :, :], bv[:, :, :], ALU.mult).then_inc(p_ok, 1)
                elif i == UNITS - 1:
                    dve.wait_ge(slo_ok, e + 1)
                    if not (isinstance(e, int) and e == 0):
                        dve.wait_ge(yS2_ok, e)
                    dve.tensor_tensor(yS[:, :], ps[0:32, 6:8, :].rearrange("p b n -> p (b n)"), slo[:, :],
                                      ALU.add).then_inc(yS_ok, 1)

            def product_lo(e, i):
                if i < 2 * NC and i % 2:
                    c = i // 2
                    dve.wait_ge(gh_ok, e * NC + (c + 1))
                    gb = g[:, 2 * c * GB:(2 * c + 2) * GB].rearrange("p (b n) -> p b n", b=2)
                    gf = gb.bitcast(F32)
                    dve.tensor_tensor(gb[:, :, 0:P], pv[:, :, 0:P], gf[:, :, P:2 * P], ALU.subtract).then_inc(gl_ok, 1)
                    dve.tensor_tensor(gb[:, :, P + C:GB], pv[:, :, P:C], gf[:, :, 2 * P:P + C], ALU.subtract).then_inc(gl_ok, 1)
            def expert(e, last):
                for i in range(1, UNITS + 1):
                    after_unit(e, i - 1)
                    if i == 26 and not last:
                        gathered_lo(e + 2)
                    n = i + SPL - 1
                    if n < UNITS:
                        split_lo(e, n)
                    elif not last:
                        split_lo(e + 1, n - UNITS)
                    product_lo(e, i - 1)

            for s in range(2):
                dve.wait_ge(xn_out[s], 16 * (TILES // 2 + 1))
                dve.wait_ge(acc_out[s], 16 * (TILES // 2 + 1))
            gathered_lo(1)
            for i in range(SPL):
                split_lo(0, i)
            expert(0, False)
            with dve.Fori(1, E - 1) as e:
                expert(e, False)
            expert(E - 1, True)

            dve.wait_ge(gfin_in, 16)
            for t in range(TILES):
                dve.wait_ge(frt_ok, t + 1)
                dve.reciprocal(frr[:, t:t + 1], fss[:, TILES + t:TILES + t + 1]).then_inc(fr_ok, 1)
                dve.wait_ge(fr_ok, t + 1)
                dve.scalar_tensor_tensor(out=fo[:, t, :], in0=fx[:, t, :], scalar=frr[:, t:t + 1], in1=gfin[:, :],
                                         op0=ALU.mult, op1=ALU.mult).then_inc(fo_ok, 1)

        @block.tensor
        def _(pe):
            pe.wait_ge(ident_ok, 4)
            for t in range(TILES):
                pe.wait_ge(xs_ok, t + 1)
                if t >= 2:
                    pe.wait_ge(hTl_ok, t - 1)
                for k in range(KD):
                    last = pe.transpose(bank(2 * (t % 2), 2)[:, k * P:(k + 1) * P], xs[:, t % 2, k * P:(k + 1) * P], ident[:, :])
                last.then_inc(xT_ps, 1)

            def project(slot):
                u = bank(3 * slot, 3)
                for k in range(KD):
                    for i, (w, h) in enumerate(((win_h, hT_h), (win_h, hT_l), (win_l, hT_h))):
                        for t0 in range(0, T, 512):
                            t1 = min(t0 + 512, T)
                            last = pe.matmul(u[:, t0:t1], w[:, slot, k, :], h[:, k, t0:t1],
                                             start=(k == 0 and i == 0), stop=(k == KD - 1 and i == 2), skip_group_check=True)
                last.then_inc(u_done, 1)

            pe.wait_ge(hTl_ok, TILES)
            with pe.Fori(0, 2) as jj:
                for q in range(6):
                    n, j = jj * 6 + q, jj * 2 + q // 3
                    pe.wait_ge(winl_ok, n + 3)
                    if q % 3 == 0:
                        pe.wait_ge(v_ok, j + 1)
                    elif q % 3 == 1:
                        pe.wait_ge(y_ok, j + 1)
                    else:
                        pe.wait_ge(uc_ok, j + 1)
                    project(q % 2)
            for j in range(JH):
                pe.wait_ge(winl_ok, 12 + j + 3)
                if j == 0:
                    pe.wait_ge(v_ok, JH + 1)
                elif j == 1:
                    pe.wait_ge(y_ok, JH + 1)
                else:
                    pe.wait_ge(ab_ok, 4 * (j - 1))
                project(j % 2)

            def norm_sums(q, col):
                for t in range(TILES):
                    last = pe.matmul(bank(7)[:, col + t:col + t + 1], q[:, t * P:(t + 1) * P], ones[:, 0:1],
                                     start=True, stop=True)
                last.then_inc(nrm_ps, 1)

            pe.wait_ge(q_ok, 1)
            norm_sums(qc, 0)

            pe.wait_ge(dd_in, 16)
            pe.wait_ge(abl_ok, JH)
            for t in range(TILES):
                if t >= 2:
                    pe.wait_ge(Yl_ok, t - 1)
                ts = slice(t * P, (t + 1) * P)
                for j in range(JH):
                    last = three(pe, bank(2 * (t % 2), 2)[:, j * 2 * P:(j + 1) * 2 * P], AB_h[:, j, ts], AB_l[:, j, ts],
                                 dd[:, 0, :], dd[:, 1, :], True, True)
                last.then_inc(dd_done, 1)

            pe.wait_ge(tab_in, 48)
            pe.wait_ge(Yl_ok, TILES)
            pe.wait_ge(rn_rt, 1)
            for j in range(JH):
                for i in range(2):
                    if j:
                        pe.wait_ge(yf_ok, 8 * (j - 1) + 2 * (i + 1))
                    for trig in range(2):
                        w = (HE, HO)[i]
                        o = i * 2 * HE + trig * w
                        cs = slice(trig * P, (trig + 1) * P)
                        for b in range(HB):
                            y = i * HB + b
                            last = three(pe, bank(4 + 2 * i + trig)[:, 0:w], Y_h[:, j, y, cs], Y_l[:, j, y, cs],
                                         tab_h[:, b, o:o + w], tab_l[:, b, o:o + w], b == 0, b == HB - 1)
                    last.then_inc(ds_done, 1)
                if j:
                    pe.wait_ge(yf_ok, 8 * j)
                for i in range(2):
                    for trig in range(2):
                        w = (SE, SO)[i]
                        o = i * 2 * SE + trig * w
                        cs = slice(trig * P, (trig + 1) * P)
                        y = 2 * HB + i
                        last = three(pe, bank(3)[:, o:o + w], Y_h[:, j, y, cs], Y_l[:, j, y, cs],
                                     tsm[:, 0, o:o + w], tsm[:, 1, o:o + w], True, True)
                last.then_inc(ds_done, 1)

            def half(t, s, h, done):
                wh, wl = ((woc_h, woc_l), (wof_h, wof_l))[h]
                for k in range(JH):
                    for n in range(2):
                        cs = slice(n * 512, (n + 1) * 512)
                        last = three(pe, bank(2 * h + n), ysh[:, s, JH * h + k, :], ysl[:, s, JH * h + k, :],
                                     wh[:, k, cs], wl[:, k, cs], k == 0, k == JH - 1)
                last.then_inc(done, 1)

            def rows(t, s, before):
                if before != "end":
                    pe.wait_ge(ysl_ok, t * 2 + 1)
                    pe.wait_ge(x1_ok, t + 1)
                    half(t, s, 0, oc_done)
                if not before:
                    pe.wait_ge(yf_ok, 8 * JH)
                    pe.wait_ge(qf_ok, 1)
                    norm_sums(qf, 16)
                if before:
                    pe.wait_ge(xn_ok, t + 2)
                    for k in range(KD):
                        last = pe.transpose(bank(4, 2)[:, k * P:(k + 1) * P], xn[:, 1 - s, k * P:(k + 1) * P], ident[:, :])
                    last.then_inc(nT_ps, 1)
                if before != "end":
                    pe.wait_ge(ysl_ok, t * 2 + 2)
                    pe.wait_ge(x2_ok, t + 1)
                    half(t, s, 1, of_done)
                if before:
                    pe.wait_ge(nT_ok, t)
                    if not (isinstance(t, int) and t == 1):
                        pe.wait_ge(lg_ok, t - 1)
                    for k in range(KD):
                        last = pe.matmul(bank(6)[:, 0:E], xnT[:, k, :], wr[:, k, :], start=(k == 0), stop=(k == KD - 1))
                    last.then_inc(lg_ps, 1)

            pe.wait_ge(wol_ok, 2 * KD)
            rows(0, 0, False)
            pe.wait_ge(gffn_in, 32)
            rows(1, 1, True)
            with pe.Fori(1, TILES // 2) as tb:
                for s in range(2):
                    rows(tb * 2 + s, s, True)
            rows(TILES, 0, "end")

            pe.wait_ge(rt_d, 5)
            for t in range(TILES):
                last = pe.transpose(psf[0:E, t * P:(t + 1) * P], aff[:, 2, t, :], ident[:, :])
            last.then_inc(rt_p, 1)
            pe.wait_ge(rt_c, 2)
            pe.transpose(bank(3)[:, 0:48], vals[:, :], ident[0:48, 0:48])
            pe.transpose(bank(3)[:, 48:96], idxf[:, :], ident[0:48, 0:48]).then_inc(rt_p, 1)

            def gathered(n):
                pe.wait_ge(xg_in[0], n * 16)
                pe.wait_ge(xg_in[1], n * 16)
                for k in range(KD):
                    o = ps[:, k // 2, (k % 2) * C:(k % 2 + 1) * C]
                    pe.transpose(o[:, 0:CAP], xg[:, k * P:(k + 1) * P], ident[:, :])
                    last = pe.transpose(o[:, CAP:C], xgs[:, k * P:(k + 1) * P], ident[0:CAPS, 0:CAPS])
                last.then_inc(xg_ps, 1)

            def expert(e, last_expert):
                for i in range(UNITS):
                    if i == 25 and not last_expert:
                        pe.wait_ge(b_ok, e * NC + NC)
                        gathered(e + 2)
                    if i == 0:
                        pe.wait_ge(xTl_ok, e + 1)
                    pe.wait_ge(sl_ok, e * UNITS + (i + 1 + RAW))
                    slot = i % SPL
                    if i < 2 * NC:
                        c = i // 2
                        if c:
                            pe.wait_ge((a_ok, b_ok)[i % 2], e * NC + c)
                        wh = spl_h[:, slot, :].rearrange("p (k f) -> p k f", k=KD)
                        wl = spl_l[:, slot, :].rearrange("p (k f) -> p k f", k=KD)
                        for b in range(2):
                            o = bank(2 * (i % 2) + b)
                            fs = slice(b * P, (b + 1) * P)
                            for k in range(KD):
                                pe.matmul(o[:, 0:2 * C], wh[:, k, fs], xT[:, k, :], start=(k == 0), stop=False,
                                          skip_group_check=True)
                                last = pe.matmul(o[:, C:2 * C], wl[:, k, fs], xT[:, k, 0:C], start=False,
                                                 stop=(k == KD - 1), skip_group_check=True)
                    else:
                        j = i - 2 * NC
                        if j == 0:
                            pe.wait_ge(yS_ok, e + 1)
                            pe.wait_ge(gl_ok, e * 2 * NC + 2 * (NC - 1))
                            if isinstance(e, int) and e == 0:
                                pe.wait_ge(gpad_ok, 1)
                            else:
                                pe.wait_ge(yP_ok, e)
                        if j == NC - 2:
                            pe.wait_ge(gl_ok, e * 2 * NC + 2 * NC)
                        for b in range(2):
                            f = 2 * j + b
                            go = f * GB
                            p_lo, p_hi, s_both = g[:, go:go + P], g[:, go + P:go + 2 * P], g[:, go + 2 * P:go + 3 * P]
                            for n in range(2):
                                ds = slice(b * D + n * 512, b * D + (n + 1) * 512)
                                wh, wl = spl_h[:, slot, ds], spl_l[:, slot, ds]
                                first, end = f == 0, f == FB - 1
                                pe.matmul(bank(4 + n), p_hi, wh, start=first, stop=False, skip_group_check=True)
                                pe.matmul(bank(4 + n), p_lo, wh, start=False, stop=False, skip_group_check=True)
                                pe.matmul(bank(4 + n), p_hi, wl, start=False, stop=end, skip_group_check=True)
                                pe.matmul(bank(6 + n), s_both, wh, start=first, stop=False, skip_group_check=True)
                                last = pe.matmul(bank(6 + n), s_both, wl, start=False, stop=end, skip_group_check=True)
                    last.then_inc(pe_unit, 1)

            gathered(1)
            expert(0, False)
            with pe.Fori(1, E - 1) as e:
                expert(e, False)
            expert(E - 1, True)


def split12(a):
    a = a.astype(np.float32)
    bits = a.view(np.uint32).astype(np.uint64)
    hi = (((bits + 0x800) >> 12) << 12).astype(np.uint32).view(np.float32)
    return hi, a - hi


def tables():
    k = np.arange(GROUP)
    ang = 2 * np.pi * (np.outer(k, k) % GROUP) / GROUP
    d = np.zeros((P, 2 * P))
    for b in range(P // GROUP):
        s = slice(b * GROUP, (b + 1) * GROUP)
        d[s, s] = np.cos(ang)
        d[s, P + b * GROUP:P + (b + 1) * GROUP] = np.sin(ang)
    dft_d = np.concatenate(split12(d), axis=1)

    def along(n):
        s = np.arange(n // 2)
        even, odd = 2 * np.arange(n // 4 + 2), 2 * np.arange(n // 4) + 1
        a, b = (2 * np.pi * (np.outer(s, f) % n) / n for f in (even, odd))
        return np.concatenate([np.cos(a), np.sin(a), np.cos(b), np.sin(b)], axis=1) / np.sqrt(n * GROUP)

    large = along(SEQ).reshape(HB, P, LARGE).transpose(1, 0, 2).reshape(P, HB * LARGE)
    dft_s = np.stack(split12(np.concatenate([large, along(DEC)], axis=1)))
    return dft_d, dft_s


_INS = ["norm_mix", "w_in", "conv_w", "g_conv", "g_fourier", "w_out", "norm_ffn", "w_router", "w_gate", "w_up",
        "w_down", "norm_final"]


def kernel(**inputs):
    import concourse.bacc as _bacc
    from concourse.bass_utils import run_bass_kernel_spmd as _run

    nc = _bacc.Bacc("TRN2", target_bir_lowering=False, num_devices=1)
    dft_d, dft_s = tables()
    named = {"x": np.concatenate([np.asarray(inputs["x_prompt"]).reshape(SEQ, D), np.asarray(inputs["x_sample"]).reshape(DEC, D)])}
    for name in _INS:
        named[name] = np.ascontiguousarray(inputs[name])
    named["dft_d"], named["dft_s"] = dft_d, dft_s
    arrays, args = {}, {}
    for name, a in named.items():
        arrays[f"in_{name}_dram"] = a
        args[name] = nc.dram_tensor(f"in_{name}_dram", a.shape, mybir.dt.from_np(a.dtype), kind="ExternalInput").ap()
    args["out"] = nc.dram_tensor("out_0_dram", (T, D), F32, kind="ExternalOutput").ap()
    build(nc, **args)
    r = _run(nc, [arrays], core_ids=[0])
    y = r.results[0]["out_0_dram"]
    return y[0:SEQ].reshape(1, SEQ, D), y[SEQ:T].reshape(1, DEC, D)
```
